# Optimizing a Trainium2 kernel written in Bass

```python
import jax, jax.numpy as jnp
from jax import lax
import numpy as np

D_MODEL = 2048
BATCH = 1
SEQ = 256
DEPTH = 1

NH_MLSTM = 4
DQK_MLSTM = 128
DV_MLSTM = 256
MLSTM_CHUNK = 128
GATE_SOFTCAP = 15.0
NH_MOBA = 8
DH_MOBA = 128
MOBA_BLOCK = 256
MOBA_TOPK = 3
MOBA_Q_CHUNK = 64
D_FF = 4 * D_MODEL
EPS = 1e-6

W_MLSTM = NH_MLSTM * DV_MLSTM
W_MOBA = NH_MOBA * DH_MOBA
IN_SIZES = (NH_MLSTM * DQK_MLSTM, NH_MLSTM * DQK_MLSTM, W_MLSTM, W_MLSTM, 2 * NH_MLSTM,
            W_MOBA, W_MOBA, W_MOBA, 2 * D_MODEL)
IN_COLS = int(sum(IN_SIZES))
IN_SPLITS = tuple(int(s) for s in np.cumsum(IN_SIZES)[:-1])

kernel_name = "hybrid_mlstm_moba_gated_block"

def rms_norm(x, g):
    xf = x.astype(jnp.float32)
    y = xf * lax.rsqrt(jnp.mean(jnp.square(xf), axis=-1, keepdims=True) + EPS)
    return y * g.astype(jnp.float32)

def soft_cap(a):
    return GATE_SOFTCAP * jnp.tanh(a / GATE_SOFTCAP)

def alibi_slopes(n_heads):
    return 2.0 ** (-8.0 * jnp.arange(1, n_heads + 1, dtype=jnp.float32) / n_heads)

def mlstm_chunkwise(q, k, v, ig, lf):
    B, H, S, dk = q.shape
    dv = v.shape[-1]
    L = MLSTM_CHUNK
    nc = S // L
    q = q * (dk ** -0.5)

    def to_chunks(a):
        return jnp.moveaxis(a.reshape((B, H, nc, L) + a.shape[3:]), 2, 0)

    causal = jnp.tril(jnp.ones((L, L), dtype=bool))

    def body(carry, xs):
        C, n, m = carry
        qc, kc, vc, igc, lfc = xs
        b = jnp.cumsum(lfc, axis=-1)
        log_d = b[..., :, None] - b[..., None, :] + igc[..., None, :]
        log_d = jnp.where(causal, log_d, -jnp.inf)
        m_inter = b + m[..., None]
        m_row = jnp.maximum(m_inter, jnp.max(log_d, axis=-1))
        s = jnp.einsum('bhld,bhsd->bhls', qc, kc) * jnp.exp(log_d - m_row[..., None])
        inter = jnp.exp(m_inter - m_row)
        num = jnp.einsum('bhls,bhsv->bhlv', s, vc) + inter[..., None] * jnp.einsum('bhld,bhdv->bhlv', qc, C)
        den = jnp.sum(s, axis=-1) + inter * jnp.einsum('bhld,bhd->bhl', qc, n)
        h = num / jnp.maximum(jnp.abs(den), jnp.exp(-m_row))[..., None]
        b_last = b[..., -1]
        log_w = b_last[..., None] - b + igc
        m_new = jnp.maximum(b_last + m, jnp.max(log_w, axis=-1))
        w = jnp.exp(log_w - m_new[..., None])
        decay = jnp.exp(b_last + m - m_new)
        C_new = decay[..., None, None] * C + jnp.einsum('bhs,bhsd,bhsv->bhdv', w, kc, vc)
        n_new = decay[..., None] * n + jnp.einsum('bhs,bhsd->bhd', w, kc)
        return (C_new, n_new, m_new), h

    carry0 = (jnp.zeros((B, H, dk, dv), jnp.float32), jnp.zeros((B, H, dk), jnp.float32),
              jnp.zeros((B, H), jnp.float32))
    _, h = lax.scan(body, carry0, (to_chunks(q), to_chunks(k), to_chunks(v), to_chunks(ig), to_chunks(lf)))
    return jnp.moveaxis(h, 0, 2).reshape(B, H, S, dv)

def moba_attention(q, k, v):
    B, H, S, dh = q.shape
    n_blk = -(-S // MOBA_BLOCK)
    s_pad = n_blk * MOBA_BLOCK
    pad = ((0, 0), (0, 0), (0, s_pad - S), (0, 0))
    q, k, v = jnp.pad(q, pad), jnp.pad(k, pad), jnp.pad(v, pad)
    kb = k.reshape(B, H, n_blk, MOBA_BLOCK, dh)
    vb = v.reshape(B, H, n_blk, MOBA_BLOCK, dh)
    k_mean = jnp.mean(kb, axis=3)
    q_blk = jnp.arange(s_pad) // MOBA_BLOCK
    fully_past = jnp.arange(n_blk)[None, :] < q_blk[:, None]
    gate = jnp.where(fully_past, jnp.einsum('bhtd,bhnd->bhtn', q, k_mean), -jnp.inf)
    top_k = min(MOBA_TOPK, n_blk)
    _, sel = lax.top_k(gate, top_k)
    slopes = alibi_slopes(H)[None, :, None, None]
    scale = dh ** -0.5
    n_qc = s_pad // MOBA_Q_CHUNK
    q_c = jnp.moveaxis(q.reshape(B, H, n_qc, MOBA_Q_CHUNK, dh), 2, 0)
    sel_c = jnp.moveaxis(sel.reshape(B, H, n_qc, MOBA_Q_CHUNK, top_k), 2, 0)
    bi = jnp.arange(B)[:, None, None, None]
    hi = jnp.arange(H)[None, :, None, None]
    blk_pos = jnp.arange(MOBA_BLOCK)

    def one_chunk(args):
        c, q_i, s_i = args
        t = c * MOBA_Q_CHUNK + jnp.arange(MOBA_Q_CHUNK)
        own = (c * MOBA_Q_CHUNK) // MOBA_BLOCK
        k_sel = kb[bi, hi, s_i]
        v_sel = vb[bi, hi, s_i]
        pos_sel = s_i[..., None] * MOBA_BLOCK + blk_pos
        dist_sel = (t[:, None, None] - pos_sel).astype(jnp.float32)
        s_sel = jnp.einsum('bhtd,bhtjsd->bhtjs', q_i, k_sel) * scale - slopes[..., None] * dist_sel
        s_sel = jnp.where((s_i < own)[..., None], s_sel, -jnp.inf)
        k_own = lax.dynamic_index_in_dim(kb, own, axis=2, keepdims=False)
        v_own = lax.dynamic_index_in_dim(vb, own, axis=2, keepdims=False)
        dist_own = (t[:, None] - (own * MOBA_BLOCK + blk_pos)[None, :]).astype(jnp.float32)
        s_own = jnp.einsum('bhtd,bhsd->bhts', q_i, k_own) * scale - slopes * dist_own
        s_own = jnp.where(dist_own >= 0, s_own, -jnp.inf)
        logits = jnp.concatenate([s_sel.reshape(B, H, MOBA_Q_CHUNK, top_k * MOBA_BLOCK), s_own], axis=-1)
        p = jax.nn.softmax(logits, axis=-1)
        p_sel = p[..., :top_k * MOBA_BLOCK].reshape(B, H, MOBA_Q_CHUNK, top_k, MOBA_BLOCK)
        p_own = p[..., top_k * MOBA_BLOCK:]
        return (jnp.einsum('bhtjs,bhtjsd->bhtd', p_sel, v_sel)
                + jnp.einsum('bhts,bhsd->bhtd', p_own, v_own))

    out = lax.map(one_chunk, (jnp.arange(n_qc), q_c, sel_c))
    return jnp.moveaxis(out, 0, 2).reshape(B, H, s_pad, dh)[:, :, :S]

def setup_inputs(seed: int = 0) -> dict:
    key = jax.random.key(seed)
    ks = jax.random.split(key, 16)

    def nrm(k, shape, scale):
        return jax.random.normal(k, shape, jnp.float32) * scale

    gate_offset = jnp.concatenate([jnp.zeros((NH_MLSTM,), jnp.float32), 3.0 * jnp.ones((NH_MLSTM,), jnp.float32)])
    return {
        "x": nrm(ks[0], (BATCH, SEQ, D_MODEL), 1.0),
        "norm_mix": 1.0 + nrm(ks[1], (DEPTH, D_MODEL), 0.02),
        "w_in": nrm(ks[2], (DEPTH, D_MODEL, IN_COLS), D_MODEL ** -0.5),
        "b_if": gate_offset + nrm(ks[3], (DEPTH, 2 * NH_MLSTM), 0.1),
        "norm_h_mlstm": 1.0 + nrm(ks[4], (DEPTH, W_MLSTM), 0.02),
        "norm_q_moba": 1.0 + nrm(ks[5], (DEPTH, DH_MOBA), 0.02),
        "norm_k_moba": 1.0 + nrm(ks[6], (DEPTH, DH_MOBA), 0.02),
        "w_branch_a": nrm(ks[7], (DEPTH, W_MLSTM, D_MODEL), W_MLSTM ** -0.5),
        "w_branch_b": nrm(ks[8], (DEPTH, W_MOBA, D_MODEL), W_MOBA ** -0.5),
        "w_out": nrm(ks[9], (DEPTH, D_MODEL, D_MODEL), D_MODEL ** -0.5),
        "norm_mlp": 1.0 + nrm(ks[10], (DEPTH, D_MODEL), 0.02),
        "w_up": nrm(ks[11], (DEPTH, D_MODEL, D_FF), D_MODEL ** -0.5),
        "w_down": nrm(ks[12], (DEPTH, D_FF, D_MODEL), D_FF ** -0.5),
    }

def reference(x, norm_mix, w_in, b_if, norm_h_mlstm, norm_q_moba, norm_k_moba,
              w_branch_a, w_branch_b, w_out, norm_mlp, w_up, w_down):
    dt = x.dtype
    B, S, _ = x.shape
    f32 = jnp.float32

    def heads(a, nh):
        return a.astype(f32).reshape(B, S, nh, -1).transpose(0, 2, 1, 3)

    for l in range(DEPTH):
        xn = rms_norm(x, norm_mix[l]).astype(dt)
        proj = xn @ w_in[l]
        qa, ka, va, oa, if_pre, qb, kb, vb, gates = jnp.split(proj, IN_SPLITS, axis=-1)

        if_pre = soft_cap(if_pre.astype(f32) + b_if[l].astype(f32))
        ig = if_pre[..., :NH_MLSTM].transpose(0, 2, 1)
        lf = jax.nn.log_sigmoid(if_pre[..., NH_MLSTM:]).transpose(0, 2, 1)
        h_a = mlstm_chunkwise(heads(qa, NH_MLSTM), heads(ka, NH_MLSTM), heads(va, NH_MLSTM), ig, lf)
        h_a = rms_norm(h_a.transpose(0, 2, 1, 3), norm_h_mlstm[l].reshape(NH_MLSTM, DV_MLSTM))
        h_a = (h_a.reshape(B, S, W_MLSTM) * jax.nn.sigmoid(oa.astype(f32))).astype(dt)

        qh = rms_norm(heads(qb, NH_MOBA), norm_q_moba[l])
        kh = rms_norm(heads(kb, NH_MOBA), norm_k_moba[l])
        h_b = moba_attention(qh, kh, heads(vb, NH_MOBA))
        h_b = h_b.transpose(0, 2, 1, 3).reshape(B, S, W_MOBA).astype(dt)

        g = jax.nn.sigmoid(gates.astype(f32))
        merged = (g[..., :D_MODEL] * (h_a @ w_branch_a[l]).astype(f32)
                  + g[..., D_MODEL:] * (h_b @ w_branch_b[l]).astype(f32)).astype(dt)
        x = x + merged @ w_out[l]

        hn = rms_norm(x, norm_mlp[l]).astype(dt)
        x = x + jnp.square(jax.nn.relu(hn @ w_up[l])) @ w_down[l]
    return x


_drawn_inputs = setup_inputs


def setup_inputs(seed=0):
    import zlib

    import numpy as np

    out = dict(_drawn_inputs(seed))
    spreads = {}
    factors = {'norm_mix': 3.754,
     'norm_h_mlstm': 8.0,
     'norm_q_moba': 8.0,
     'norm_k_moba': 8.0,
     'norm_mlp': 3.283}
    for name, (base, spread) in spreads.items():
        noise = np.random.default_rng([zlib.crc32(name.encode()), seed]).standard_normal(out[name].shape)
        drawn = base * np.exp(spread * noise) if base else spread * noise
        out[name] = __import__('jax').numpy.asarray(drawn.astype(out[name].dtype))
    for name, factor in factors.items():
        out[name] = (out[name] * factor).astype(out[name].dtype)
    return out
```

```python
from contextlib import ExitStack

import concourse.bass as bass
from concourse import mybir

P = 128
S, D, FF = 256, 2048, 8192
M = S // P
NA, DK, DV = 4, 128, 256
NB, DH = 8, 128
L = 128
CAP = 15.0
EPS = 1e-6
N = 512
KT = D // P
KL = 4
KH = 2
RAW = 4
RING = 4
IF = 2 * NA
IF_COL = 2 * NA * DK + 2 * NA * DV
B_COL = IF_COL + IF
G_COL = B_COL + 3 * NB * DH
W_IN_COLS = [B_COL + N * i for i in range(6)] + [N * i for i in range(6)]
N_WIN = len(W_IN_COLS)
NN = D // N
B_BRANCH = N_WIN
B_OUT = B_BRANCH + 3 * NN
B_UP = B_OUT + NN
FB = 16
MASKED = 30000.0
FAR = 1.0e30

F32 = mybir.dt.float32
F32R = mybir.dt.float32r
I32 = mybir.dt.int32
ALU = mybir.AluOpType
ACT = mybir.ActivationFunctionType
AX = mybir.AxisListType.X

QK_BLOCKS = [0, 1, 2, 3, 6, 7]
P_IF_SUM, P_IF_ADD, P_IF_ROWS, P_IF_COLS = 9, 14, 25, 42


def p_moba(h):
    return 46 + 4 * h


def p_mlstm(h):
    return 80 + 4 * h


def p_sv(h):
    return 94 + 3 * h


P_HA = 112


def build(nc, x, norm_mix, w_in, b_if, norm_h, norm_q, norm_k, w_a, w_b, w_out, norm_mlp, w_up, w_down, out):
    w_in_t = w_in[0].rearrange("(t p) n -> p t n", p=P)
    w_a_t = w_a[0].rearrange("(t p) n -> p t n", p=P)
    w_b_t = w_b[0].rearrange("(t p) n -> p t n", p=P)
    w_out_t = w_out[0].rearrange("(t p) n -> p t n", p=P)
    w_up_t = w_up[0].rearrange("(t p) n -> p t n", p=P)
    w_down_t = w_down[0].rearrange("(t p) n -> p t n", p=P)
    x_t = x[0].rearrange("(m p) n -> p m n", p=P)
    out_t = out[0].rearrange("(m p) n -> p m n", p=P)

    with ExitStack() as ctx:
        def sb(name, shape, dt=F32):
            return ctx.enter_context(nc.sbuf_tensor(name, shape, dt))

        def sem(name):
            return ctx.enter_context(nc.semaphore(name))

        raw = sb("raw", [P, RAW, KL, N])
        w_hi = sb("w_hi", [P, RING, KH, N], F32R)
        w_lo = sb("w_lo", [P, RING, KH, N], F32R)
        xT = sb("xT", [P, KT, 2, S], F32R)
        branch = sb("branch", [P, 16, 2, S], F32R)
        with nc.sbuf_tensor("attn", [P, 8192], F32) as attn:
            pass
        merged = sb("merged", [P, 16, 2, S], F32R)
        qTb = attn[:, 0:2048].rearrange("p (h t) -> p h t", h=NB)
        kTb = attn[:, 2048:4096].rearrange("p (h t) -> p h t", h=NB)
        vb = attn[:, 4096:6144].rearrange("p (m c) -> p m c", m=M)
        nat = [attn[:, 6144 + 1024 * i:7168 + 1024 * i].rearrange("p (m c) -> p m c", m=M) for i in range(2)]
        num = attn[:, 4096:6144].rearrange("p (m h c) -> p m h c", m=M, h=NA)
        wt = attn[:, 6144:6144 + 4 * 384].rearrange("p (h c) -> p h c", h=NA)
        rows = sb("rows", [P, M, D])
        va = rows[:, :, 0:NA * DV]
        oa = rows[:, :, NA * DV:2 * NA * DV]
        qTa = sb("qTa", [P, NA, S])
        kTa = sb("kTa", [P, NA, S])
        gate = sb("gate", [P, 2, M, N])
        gate_f = gate[:, :, :, :].rearrange("p a m n -> p (a m n)")
        sq = gate_f[:, 0:1024]
        e_t = gate_f[:, 0:768].rearrange("p (b c) -> p b c", b=2)
        up_lo = gate_f[:, 0:1024].rearrange("p (j t) -> p j t", j=4)
        up_sq = gate_f[:, 1024:2048].rearrange("p (j t) -> p j t", j=4)
        prob = sb("prob", [P, 2, 384])
        probT = sb("probT", [P, 2, 384])
        prob_f = prob[:, :, :].rearrange("p b c -> p (b c)")
        probT_f = probT[:, :, :].rearrange("p b c -> p (b c)")
        ident = sb("ident", [P, P])
        dist = sb("dist", [P, 384])
        dist_i = prob[:, 0, :].bitcast(I32)
        late = sb("late", [P, P])
        pick = sb("pick", [NA, NA, P])
        add2 = sb("add2", [16, IF])
        ones = sb("ones", [P, 2])
        mix_rows = sb("mix_rows", [16, P])
        g_rows = sb("g_rows", [26, P])
        warm = sb("warm", [P, 1])
        g_col = sb("g_col", [P, 42])
        G_MIX, G_MLP, G_H, G_Q, G_K = 0, 16, 32, 40, 41
        bias_i = sb("bias_i", [NA, 1])
        bias_f = sb("bias_f", [NA, 1])
        wif = sb("wif", [P, KT, IF])
        wif2 = sb("wif2", [P, KT * 16 + 112], F32R)
        half_pow = sb("half_pow", [P, 8])
        ssq = sb("ssq", [P, 8])
        rms = sb("rms", [P, 8])
        x_ss = sb("x_ss", [P, M])
        rstd = sb("rstd", [P, M])
        low = sb("low", [P, 2, M])
        psum_p = sb("psum_p", [P, 2, M])
        psum_r = sb("psum_r", [P, 2, M])
        if_nat = sb("if_nat", [P, M, IF])
        if_raw = rows[0:16, 0, 1024:1536].rearrange("p (a t) -> p a t", a=2)
        gi = rows[0:NA, 0, 1536:2048].rearrange("p (a t) -> p a t", a=2)
        t_e, t_l, lf, bcum = (rows[0:NA, 1, 1024 + S * i:1024 + S * i + S] for i in range(4))
        a_r, g_r, m_r = (gate_f[0:NA, 1024 + S * i:1024 + S * i + S] for i in range(3))
        lw_r = gate_f[0:NA, 1024 + 3 * S:1024 + 3 * S + L]
        m1 = sb("m1", [NA, 1])
        ones_r = sb("ones_r", [NA, L])
        cols = sb("cols", [P, 5, NA])
        floor = sb("floor", [P, M, NA])
        den = sb("den", [P, M, NA])
        den_r = sb("den_r", [P, M, NA])
        num_ss = sb("num_ss", [P, M, NA])
        h_rms = sb("h_rms", [P, M, NA])
        h_fac = sb("h_fac", [P, M, NA])
        x2_ss = sb("x2_ss", [P, M, NN])
        x2_ms = sb("x2_ms", [P, M])
        x2_q = sb("x2_q", [P, M])

        ps = ctx.enter_context(nc.psum_tensor("ps", [P, 8, 512], F32))

        def banks(a, b):
            return ps[:, a:b, :].rearrange("p b c -> p (b c)")

        landed = [sem(f"landed{i}") for i in range(RAW)]
        slot_clear = sem("slot_clear")
        hi_made, lo_made, w_used = sem("hi_made"), sem("lo_made"), sem("w_used")
        kept = [sem("kept0"), sem("kept1")]
        mix_landed, c_landed, wif_landed, c_pool, g_turned, g_kept = (
            sem(s) for s in ("mix_landed", "c_landed", "wif_landed", "c_pool", "g_turned", "g_kept"))
        first_landed = sem("first_landed")
        x_landed = [sem(f"x_landed{i}") for i in range(8)]
        x_turned, xh_made, xl_made, x_summed, rstd_made = (
            sem(s) for s in ("x_turned", "xh_made", "xl_made", "x_summed", "rstd_made"))
        ss_made, rms_made, nat_scaled, qk_turned, qk_kept = (
            sem(s) for s in ("ss_made", "rms_made", "nat_scaled", "qk_turned", "qk_kept"))
        if_hi, if_lo, if_pe, if_act, if_dve = (sem(s) for s in ("if_hi", "if_lo", "if_pe", "if_act", "if_dve"))
        sc_made, low_made, p_made, p_scaled, p_turned, pt_kept, hb_made, hb_hi, hb_lo = (
            sem(s) for s in ("sc_made", "low_made", "p_made", "p_scaled", "p_turned", "pt_kept",
                             "hb_made", "hb_hi", "hb_lo"))
        st_made, arg_made, e_made, wt_made, sv_made, num_kept, den_kept, hr_in, hr_made, ha_made, ha_turned, ha_hi, \
            ha_lo = (sem(s) for s in ("st_made", "arg_made", "e_made", "wt_made", "sv_made", "num_kept", "den_kept",
                                      "hr_in", "hr_made", "ha_made", "ha_turned", "ha_hi", "ha_lo"))
        mg_made, mg_turned, mg_hi, mg_lo = (sem(s) for s in ("mg_made", "mg_turned", "mg_hi", "mg_lo"))
        xr_landed, x2_summed, x2_turned, x2_hi, x2_lo = (
            sem(s) for s in ("xr_landed", "x2_summed", "x2_turned", "x2_hi", "x2_lo"))
        up_kept, up_read, up_squared, up_hi, up_lo_made = (
            sem(s) for s in ("up_kept", "up_read", "up_squared", "up_hi", "up_lo_made"))
        down_m0 = sem("down_m0")
        down_read, stored = sem("down_read"), sem("stored")
        dve_step, pool_step = sem("dve_step"), sem("pool_step")

        block = ctx.enter_context(nc.Block())

        def hn(n):
            return 8 * (B_BRANCH + 3 * n)

        @block.sync
        def _(sp):
            def load(blk, k, src):
                if not isinstance(blk, int) or blk >= 1:
                    sp.wait_ge(lo_made, 8 * blk - 8 + 2 * k + 2)
                    if not isinstance(blk, int):
                        sp.sem_inc(slot_clear, 1)
                sp.dma_start(raw[:, k, :, :], src).then_inc(landed[k], 16)

            first = slice(W_IN_COLS[0], W_IN_COLS[0] + N)
            for k in range(8):
                c = slice(2 * P * k, 2 * P * k + 2 * P)
                sp.dma_start(rows[:, :, c], x_t[:, :, c]).then_inc(x_landed[k], 16)
                if k == 0:
                    sp.dma_start(raw[:, 0, 0:KH, :], w_in_t[:, 0:KH, first]).then_inc(first_landed, 16)
                if k == 1:
                    sp.dma_start(raw[:, 0, KH:KL, :], w_in_t[:, KH:KL, first]).then_inc(landed[0], 16)
                if k in (3, 5, 7):
                    load(0, k // 2, w_in_t[:, KL * (k // 2):KL * (k // 2) + KL, first])
            for b in range(1, N_WIN):
                for k in range(4):
                    load(b, k, w_in_t[:, KL * k:KL * k + KL, W_IN_COLS[b]:W_IN_COLS[b] + N])

            def branch_loads(n):
                blk = B_BRANCH + 3 * n
                for g in range(2):
                    for k in range(4):
                        load(blk + g, k, w_in_t[:, KL * k:KL * k + KL, bass.ds(G_COL + D * g + N * n, N)])
                for k in range(4):
                    w = w_b_t if k < 2 else w_a_t
                    load(blk + 2, k, w[:, KL * (k % 2):KL * (k % 2) + KL, bass.ds(N * n, N)])

            branch_loads(0)
            sp.wait_ge(ha_turned, 1)
            sp.dma_start(rows[:, :, :], x_t).then_inc(xr_landed, 16)
            with sp.Fori(1, NN) as n:
                branch_loads(n)
            with sp.Fori(0, NN) as n:
                for k in range(4):
                    load(B_OUT + n, k, w_out_t[:, KL * k:KL * k + KL, bass.ds(N * n, N)])
            for f in range(2):
                with sp.Fori(0, 8) as j:
                    for k in range(4):
                        load(B_UP + FB * f + j, k, w_up_t[:, KL * k:KL * k + KL, bass.ds(4096 * f + N * j, N)])
                with sp.Fori(0, NN) as n:
                    for k in range(8):
                        load(B_UP + FB * f + 8 + 2 * n + k // 4, k % 4,
                             w_down_t[:, 32 * f + KL * k:32 * f + KL * k + KL, bass.ds(N * n, N)])
            for n in range(NN):
                for m in range(M):
                    sp.wait_ge(down_read, M * (NN + n) + m + 1)
                    sp.dma_start(out_t[:, m, N * n:N * n + N], rows[:, m, N * n:N * n + N]).then_inc(stored, 16)
            sp.wait_ge(stored, 16 * NN * M)

        @block.gpsimd
        def _(pool):
            steps = [0]

            def link(ins):
                steps[0] += 1
                ins.then_inc(pool_step, 1)
                pool.wait_ge(pool_step, steps[0])

            link(pool.memset(ident[:, :], 0.0))
            pool.affine_select(out=ident[:, :], in_=ident[:, :], compare_op=ALU.not_equal, fill=1.0, base=0,
                               pattern=[[-1, P]], channel_multiplier=1).then_inc(c_pool, 1)
            pool.memset(half_pow[:, :], -0.5)
            pool.memset(ones[:, :], 1.0)
            pool.memset(ones_r[:, :], 1.0)
            pool.memset(late[:, :], 0.0)
            pool.memset(pick[:, :, :], 0.0)
            link(pool.memset(add2[:, :], 0.0))
            pool.affine_select(out=late[:, :], in_=late[:, :], compare_op=ALU.is_ge, fill=MASKED, base=0,
                               pattern=[[1, P]], channel_multiplier=-1)
            pool.affine_select(out=pick[:, :, :], in_=pick[:, :, :], compare_op=ALU.not_equal, fill=1.0, base=0,
                               pattern=[[-1, NA], [0, P]], channel_multiplier=1)
            link(pool.affine_select(out=add2[:, :], in_=add2[:, :], compare_op=ALU.not_equal, fill=1.0, base=0,
                                    pattern=[[-1, IF]], channel_multiplier=1))
            link(pool.affine_select(out=add2[:, :], in_=add2[:, :], compare_op=ALU.not_equal, fill=1.0, base=-IF,
                                    pattern=[[-1, IF]], channel_multiplier=1))
            pool.iota(dist_i[:, 0:128], pattern=[[-1, P]], base=0, channel_multiplier=1)
            pool.iota(dist_i[:, 128:256], pattern=[[-1, P]], base=P, channel_multiplier=1)
            link(pool.iota(dist_i[:, 256:384], pattern=[[-1, P]], base=0, channel_multiplier=1))
            link(pool.tensor_copy(dist[:, :], dist_i[:, :]))
            for c in (0, 256):
                last = pool.affine_select(out=dist[:, c:c + P], in_=dist[:, c:c + P], compare_op=ALU.is_ge, fill=FAR,
                                          base=0, pattern=[[-1, P]], channel_multiplier=1)
            last.then_inc(c_pool, 1)

            def inverse_rms(out_ap, sum_ap, count, done):
                link(pool.tensor_scalar(sum_ap, sum_ap, 1.0 / count, EPS, ALU.mult, ALU.add))
                w = sum_ap.shape[-1]
                pool.tensor_tensor(out_ap, sum_ap, half_pow[:, 0:w], ALU.pow).then_inc(done, 1)

            pool.wait_ge(x_summed, M)
            inverse_rms(rstd[:, :], x_ss[:, :], D, rstd_made)
            for i in range(4):
                pool.wait_ge(ss_made, i + 1)
                if i >= 1:
                    pool.wait_ge(nat_scaled, i)
                inverse_rms(rms[:, :], ssq[:, :], DH, rms_made)
            pool.wait_ge(hr_in, 1)
            inverse_rms(h_rms[:, :, :].rearrange("p m h -> p (m h)"), num_ss[:, :, :].rearrange("p m h -> p (m h)"),
                        DV, hr_made)

        @block.scalar
        def _(act):
            act.dma_start(mix_rows[:, :], norm_mix[0].rearrange("(t p) -> t p", p=P)).then_inc(mix_landed, 16)

            def load_constants():
                act.dma_start(g_rows[0:16, :], norm_mlp[0].rearrange("(t p) -> t p", p=P)).then_inc(c_landed, 16)
                act.dma_start(g_rows[16:24, :], norm_h[0].rearrange("(t p) -> t p", p=P)).then_inc(c_landed, 16)
                act.dma_start(g_rows[24:25, :], norm_q).then_inc(c_landed, 16)
                act.dma_start(g_rows[25:26, :], norm_k).then_inc(c_landed, 16)
                act.dma_start(bias_i[:, :], b_if[0, 0:NA].rearrange("(h a) -> h a", a=1)).then_inc(c_landed, 16)
                act.dma_start(bias_f[:, :], b_if[0, NA:IF].rearrange("(h a) -> h a", a=1)).then_inc(c_landed, 16)
                act.dma_start(wif[:, :, :], w_in_t[:, :, IF_COL:IF_COL + IF]).then_inc(wif_landed, 16)

            def split_hi(blk, k):
                if isinstance(blk, int) and 8 * blk + k == 0:
                    act.wait_ge(first_landed, 16)
                else:
                    act.wait_ge(landed[k // 2], 16 * blk + 16)
                if not isinstance(blk, int) or 8 * blk + k >= RING:
                    act.wait_ge(w_used, 8 * blk + k - RING + 1)
                act.activation(w_hi[:, k % RING, :, :], raw[:, k // 2, KH * (k % 2):KH * (k % 2) + KH, :],
                               ACT.Copy).then_inc(hi_made, 1)

            def keep_rows(g, dst, func=ACT.Copy):
                act.wait_ge(w_used, 8 * g + 8)
                for m in range(M):
                    last = act.activation(dst[:, m, :], ps[:, 2 * (g % 2) + m, :], func, scale=rstd[:, m:m + 1])
                last.then_inc(kept[g % 2], 1)

            def exps_moba(h):
                act.wait_ge(low_made, h + 1)
                if h >= 2:
                    act.wait_ge(p_turned, h - 1)
                act.activation(prob[:, h % 2, 0:128], prob[:, h % 2, 0:128], ACT.Exp, scale=-1.0,
                               bias=low[:, h % 2, 0:1], accum_out=psum_p[:, h % 2, 0:1])
                act.activation(prob[:, h % 2, 128:384], prob[:, h % 2, 128:384], ACT.Exp, scale=-1.0,
                               bias=low[:, h % 2, 1:2], accum_out=psum_p[:, h % 2, 1:2]).then_inc(p_made, 1)

            def exps_mlstm(h):
                act.wait_ge(arg_made, h + 1)
                e = e_t[:, h % 2, :]
                diag = e.rearrange("p (b c) -> p b c", c=128)[:, 0:3:2, :]
                act.activation(diag, diag, ACT.Exp, scale=-1.0)
                act.activation(e[:, 128:256], ps[:, 4, 128:256], ACT.Exp, scale=-1.0,
                               bias=cols[:, 2, h:h + 1]).then_inc(e_made, 1)

            def jobs(H):
                if H in (9, 11):
                    m = (H - 9) // 2
                    for q in range(8):
                        act.wait_ge(x_landed[q], 16)
                    if m == 1:
                        act.wait_ge(x_summed, 1)
                    act.activation(gate_f[:, :], rows[:, m, :], ACT.Square,
                                   accum_out=x_ss[:, m:m + 1]).then_inc(x_summed, 1)
                if H == 7:
                    act.wait_ge(wif_landed, 16)
                    act.wait_ge(if_dve, 1)
                    act.activation(wif2[:, 0:KT * 16].rearrange("p (t c) -> p t c", c=16)[:, :, 0:IF], wif[:, :, :],
                                   ACT.Copy).then_inc(if_hi, 1)
                if H == P_IF_SUM + 5:
                    act.wait_ge(if_pe, 1)
                    act.activation(if_raw[:, :, :], ps[0:16, 7, :].rearrange("p (a t) -> p a t", a=2),
                                   ACT.Copy).then_inc(if_act, 1)
                if H == P_IF_ROWS + 6:
                    act.wait_ge(if_dve, 3)
                    act.activation(gi[:, :, :], gi[:, :, :], ACT.Tanh).then_inc(if_act, 1)
                if H == P_IF_ROWS + 8:
                    act.wait_ge(if_dve, 4)
                    act.activation(t_e[:, :], t_e[:, :], ACT.Exp, scale=-1.0).then_inc(if_act, 1)
                    act.wait_ge(if_act, 3)
                    act.activation(t_l[:, :], t_e[:, :], ACT.Ln, bias=1.0).then_inc(if_act, 1)
                if H == P_IF_COLS + 6:
                    act.wait_ge(if_dve, 6)
                    act.activation(floor[:, :, :], cols[:, 3:5, :], ACT.Exp, scale=-1.0).then_inc(if_act, 1)
                for b in range(N_WIN):
                    if H != 8 * b + 12:
                        continue
                    if b == 0:
                        act.wait_ge(rstd_made, 1)
                    if b < 4 or b in (6, 7):
                        if b >= 2:
                            act.wait_ge(qk_turned, {2: 1, 3: 2, 6: 3, 7: 4}[b])
                        keep_rows(b, nat[b % 2])
                    elif b < 6:
                        keep_rows(b, vb[:, :, N * (b - 4):N * (b - 4) + N])
                    elif b < 10:
                        keep_rows(b, va[:, :, N * (b - 8):N * (b - 8) + N])
                    else:
                        keep_rows(b, oa[:, :, N * (b - 10):N * (b - 10) + N], ACT.Sigmoid)
                for i in range(4):
                    if H == 8 * i + 17:
                        act.wait_ge(qk_turned, i + 1)
                        act.wait_ge(g_kept, 2)
                        src = banks(4 + 2 * (i % 2), 6 + 2 * (i % 2)).rearrange("p (h t) -> p h t", h=4)
                        dst, g = (qTb, G_Q) if i < 2 else (kTb, G_K)
                        act.activation(dst[:, 4 * (i % 2):4 * (i % 2) + 4, :], src, ACT.Copy,
                                       scale=g_col[:, g:g + 1]).then_inc(qk_kept, 1)
                for i in range(4):
                    if H == 65 + 5 * i:
                        act.wait_ge(qk_turned, 5 + i)
                        dst = qTa if i < 2 else kTa
                        act.activation(dst[:, 2 * (i % 2):2 * (i % 2) + 2, :],
                                       ps[:, 7, :].rearrange("p (h t) -> p h t", h=2), ACT.Copy,
                                       scale=DK ** -0.5 if i < 2 else 1.0).then_inc(qk_kept, 1)
                for h in range(NB):
                    if H == p_moba(h) + 6:
                        exps_moba(h)
                    if H == p_moba(h) + 12:
                        act.wait_ge(p_turned, h + 1)
                        if h >= 2:
                            act.wait_ge(hb_made, h - 1)
                        act.activation(probT[:, h % 2, :], ps[:, 5, 0:384], ACT.Copy).then_inc(pt_kept, 1)
                    if H == p_moba(h) + 18:
                        act.wait_ge(hb_made, h + 1)
                        act.activation(branch[:, NB + h, 0, :], ps[:, 6, 0:S], ACT.Copy).then_inc(hb_hi, 1)
                for h in range(NA):
                    if H == p_mlstm(h) + 6:
                        exps_mlstm(h)
                    if H == p_sv(h) + 5:
                        act.wait_ge(sv_made, h + 1)
                        if h == 0:
                            act.wait_ge(hb_made, NB)
                        act.activation(num[:, :, h, :], ps[:, 5:7, 0:DV], ACT.Copy)
                        for m in range(M):
                            last = act.activation(probT[:, m, 0:DV], ps[:, 5 + m, 0:DV], ACT.Square,
                                                  accum_out=num_ss[:, m, h:h + 1])
                        last.then_inc(num_kept, 1)
                if H == P_HA + 5:
                    act.wait_ge(ha_turned, 1)
                    for t in range(8):
                        last = act.activation(branch[:, t, 0, :], ps[:, 4 + t // 2, S * (t % 2):S * (t % 2) + S],
                                              ACT.Copy, scale=g_col[:, G_H + t:G_H + t + 1])
                    last.then_inc(ha_hi, 1)

            def keep_gate(n, a):
                if not isinstance(n, int):
                    act.wait_ge((mg_turned, mg_made)[a], n)
                act.wait_ge(w_used, 8 * (B_BRANCH + 3 * n + a) + 8)
                for m in range(M):
                    last = act.activation(gate[:, a, m, :], ps[:, 2 * a + m, :], ACT.Sigmoid, scale=rstd[:, m:m + 1])
                last.then_inc(kept[a], 1)

            def merged_hi(n):
                act.wait_ge(mg_turned, n + 1)
                act.activation(merged[:, bass.ds(4 * n, 4), 0, :], banks(4, 6).rearrange("p (t c) -> p t c", t=4),
                               ACT.Copy).then_inc(mg_hi, 1)

            act.wait_ge(c_pool, 1)
            act.activation(warm[:, :], ident[:, 0:1], ACT.Copy)
            act.wait_ge(g_kept, 1)
            for k in range(8):
                if k == 1:
                    load_constants()
                act.wait_ge(x_turned, k + 1)
                for t in range(2 * k, 2 * k + 2):
                    last = act.activation(xT[:, t, 0, :], ps[:, 4 + k % 4, S * (t % 2):S * (t % 2) + S], ACT.Copy,
                                          scale=g_col[:, G_MIX + t:G_MIX + t + 1])
                last.then_inc(xh_made, 1)
                if k == 7:
                    jobs(7)
                split_hi(0, k)
            for H in range(8, hn(0) + 8):
                jobs(H)
                split_hi(H // 8, H % 8)
            for H in range(hn(0) + 8, hn(1) + 8):
                jobs(H)
                if H == hn(0) + 12:
                    keep_gate(0, 0)
                if H == hn(0) + 20:
                    keep_gate(0, 1)
                if H == hn(0) + 31:
                    merged_hi(0)
                split_hi(H // 8, H % 8)
            with act.Fori(1, NN) as n:
                for i in range(8, 32):
                    if i == 12:
                        keep_gate(n, 0)
                    if i == 20:
                        keep_gate(n, 1)
                    if i == 31:
                        merged_hi(n)
                    split_hi(B_BRANCH + 3 * n + i // 8, i % 8)
            for H in range(8 * B_OUT + 8, 8 * B_UP + 12):
                for i in range(NN):
                    if H == 8 * (B_OUT + i) + 13:
                        act.wait_ge(kept[i % 2], 15 + i // 2)
                        if i >= 1:
                            act.wait_ge(x2_summed, i)
                        for m in range(M):
                            last = act.activation((prob_f, probT_f)[m][:, 0:N], rows[:, m, N * i:N * i + N], ACT.Square,
                                                  accum_out=x2_ss[:, m, i:i + 1])
                        last.then_inc(x2_summed, 1)
                    if H == 8 * (B_OUT + i) + 15:
                        act.wait_ge(x2_turned, i + 1)
                        b0 = 4 if i < 3 else 0
                        for t in range(4):
                            last = act.activation(xT[:, 4 * i + t, 0, :],
                                                  ps[:, b0 + t // 2, S * (t % 2):S * (t % 2) + S], ACT.Copy,
                                                  scale=g_col[:, G_MLP + 4 * i + t:G_MLP + 4 * i + t + 1])
                        last.then_inc(x2_hi, 1)
                split_hi(H // 8, H % 8)
            feats = [branch, merged]
            for f in range(2):
                blk0 = B_UP + FB * f
                for half in range(2):
                    feat = feats[half]
                    with act.Fori(0, 2) as jj:
                        for u in range(2):
                            j = 4 * half + 2 * jj + u
                            q0 = 4 * ((u + 1) % 2)
                            act.wait_ge(w_used, 8 * (blk0 + j) + 8)
                            act.activation(up_lo, ps[:, q0:q0 + 4, S:2 * S], ACT.Copy).then_inc(up_kept, 1)
                            for i in range(12, 20):
                                if i == 14:
                                    act.wait_ge(up_squared, 8 * f + j + 1)
                                    act.activation(feat[:, bass.ds(4 * (2 * jj + u), 4), 0, :], up_sq,
                                                   ACT.Copy).then_inc(up_hi, 1)
                                split_hi(blk0 + j + i // 8, i % 8)
                with act.Fori(0, NN if f == 0 else 3) as n:
                    for i in range(12, 28):
                        split_hi(blk0 + 8 + 2 * n + i // 8, i % 8)
                if f == 1:
                    for k in range(4, 8):
                        split_hi(blk0 + 15, k)

        @block.vector
        def _(dve):
            steps = [0]

            def link(ins):
                steps[0] += 1
                ins.then_inc(dve_step, 1)
                dve.wait_ge(dve_step, steps[0])

            def split_lo(blk, k):
                dve.wait_ge(hi_made, 8 * blk + k + 1)
                dve.tensor_tensor(w_lo[:, k % RING, :, :], raw[:, k // 2, KH * (k % 2):KH * (k % 2) + KH, :],
                                  w_hi[:, k % RING, :, :].bitcast(F32), ALU.subtract).then_inc(lo_made, 1)

            def turned_lo(dst, tiles, b0, gain):
                for i, t in enumerate(tiles):
                    last = dve.scalar_tensor_tensor(
                        out=dst[:, t, 1, :], in0=ps[:, b0 + i // 2, S * (i % 2):S * (i % 2) + S],
                        scalar=g_col[:, gain + i:gain + i + 1], in1=dst[:, t, 0, :].bitcast(F32),
                        op0=ALU.mult, op1=ALU.subtract)
                return last

            def if_rows():
                lo, hi = slice(0, L), slice(L, 2 * L)
                link(dve.scalar_tensor_tensor(out=lf[:, :], in0=gi[:, 1, :], scalar=0.0, in1=t_l[:, :],
                                              op0=ALU.min, op1=ALU.subtract))
                for c in (lo, hi):
                    link(dve.tensor_tensor_scan(bcum[:, c], ones_r[:, :], lf[:, c], 0.0, ALU.mult, ALU.add))
                link(dve.tensor_tensor(a_r[:, :], gi[:, 0, :], bcum[:, :], ALU.subtract))
                link(dve.tensor_tensor_scan(g_r[:, lo], a_r[:, lo], a_r[:, lo], 0.0, ALU.max, ALU.max))
                link(dve.tensor_scalar(lw_r[:, :], a_r[:, lo], bcum[:, L - 1:L], None, ALU.add))
                link(dve.tensor_tensor(m1[:, :], bcum[:, L - 1:L], g_r[:, L - 1:L], ALU.add))
                link(dve.tensor_tensor_scan(g_r[:, hi], a_r[:, hi], a_r[:, hi], m1[:, 0:1], ALU.max, ALU.max))
                dve.tensor_tensor(m_r[:, :], bcum[:, :], g_r[:, :], ALU.add).then_inc(if_dve, 1)

            def jobs(H):
                if H == 8:
                    dve.wait_ge(g_turned, 2)
                    link(dve.tensor_copy(g_col[:, 16:42], ps[:, 3, 16:42]))
                    dve.tensor_scalar(g_col[:, G_Q:G_Q + 1], g_col[:, G_Q:G_Q + 1], DH ** -0.5, None,
                                      ALU.mult).then_inc(g_kept, 1)
                if H == 8:
                    dve.wait_ge(if_hi, 1)
                    w = wif2[:, 0:KT * 16].rearrange("p (t c) -> p t c", c=16)
                    dve.tensor_tensor(w[:, :, IF:16], wif[:, :, :], w[:, :, 0:IF].bitcast(F32),
                                      ALU.subtract).then_inc(if_lo, 1)
                for i in range(4):
                    n3 = nat[i % 2].rearrange("p m (h c) -> p (m h) c", c=DH)
                    if H == 8 * i + 12:
                        dve.wait_ge(kept[i % 2], i // 2 + 1)
                        nf = nat[i % 2].rearrange("p m c -> p (m c)")
                        link(dve.tensor_tensor(sq, nf, nf, ALU.mult))
                        if i >= 1:
                            dve.wait_ge(rms_made, i)
                        dve.tensor_reduce(ssq[:, :], sq.rearrange("p (g c) -> p g c", c=DH), AX,
                                          ALU.add).then_inc(ss_made, 1)
                    if H == 8 * i + 14:
                        dve.wait_ge(rms_made, i + 1)
                        dve.tensor_tensor(n3, n3, rms[:, :].unsqueeze(2).to_broadcast([P, 8, DH]),
                                          ALU.mult).then_inc(nat_scaled, 1)
                if H == P_IF_ADD + 5:
                    dve.wait_ge(if_pe, 2)
                    for m in range(M):
                        last = dve.tensor_scalar(if_nat[:, m, :], ps[:, 7, IF * m:IF * m + IF], rstd[:, m:m + 1], None,
                                                 ALU.mult)
                    last.then_inc(if_dve, 1)
                if H == P_IF_ROWS + 5:
                    dve.wait_ge(if_pe, 3)
                    for a, bias in enumerate((bias_i, bias_f)):
                        last = dve.tensor_scalar(gi[:, a, :], ps[0:NA, 7, S * a:S * a + S], bias[:, 0:1], 1.0 / CAP,
                                                 ALU.add, ALU.mult)
                    last.then_inc(if_dve, 1)
                if H == P_IF_ROWS + 7:
                    dve.wait_ge(if_act, 2)
                    link(dve.tensor_scalar(gi[:, :, :], gi[:, :, :], CAP, None, ALU.mult))
                    dve.scalar_tensor_tensor(out=t_e[:, :], in0=gi[:, 1, :], scalar=-1.0, in1=gi[:, 1, :],
                                             op0=ALU.mult, op1=ALU.max).then_inc(if_dve, 1)
                if H == P_IF_ROWS + 9:
                    dve.wait_ge(if_act, 4)
                    if_rows()
                if H == P_IF_COLS + 5:
                    dve.wait_ge(if_pe, 4)
                    dve.tensor_copy(cols[:, :, :], ps[:, 7, 0:5 * NA].rearrange("p (a h) -> p a h", h=NA))\
                       .then_inc(if_dve, 1)
                for h in range(NB):
                    pr = prob[:, h % 2, :]
                    if H == p_moba(h) + 5:
                        dve.wait_ge(sc_made, h + 1)
                        if h == 0:
                            dve.wait_ge(c_pool, 2)
                        else:
                            if h >= 2:
                                dve.wait_ge(p_turned, h - 1)
                        link(dve.scalar_tensor_tensor(out=pr, in0=dist[:, :], scalar=2.0 ** (-8.0 * (h + 1) / NB),
                                                      in1=ps[:, 4, 0:384], op0=ALU.mult, op1=ALU.subtract))
                        dve.tensor_reduce(low[:, h % 2, 0:1], pr[:, 0:128], AX, ALU.min)
                        dve.tensor_reduce(low[:, h % 2, 1:2], pr[:, 128:384], AX, ALU.min).then_inc(low_made, 1)
                    if H == p_moba(h) + 7:
                        dve.wait_ge(p_made, h + 1)
                        link(dve.reciprocal(psum_r[:, h % 2, :], psum_p[:, h % 2, :]))
                        dve.tensor_scalar(pr[:, 0:128], pr[:, 0:128], psum_r[:, h % 2, 0:1], None, ALU.mult)
                        dve.tensor_scalar(pr[:, 128:384], pr[:, 128:384], psum_r[:, h % 2, 1:2], None,
                                          ALU.mult).then_inc(p_scaled, 1)
                    if H == p_moba(h) + 18:
                        dve.wait_ge(hb_hi, h + 1)
                        dve.tensor_tensor(branch[:, NB + h, 1, :], ps[:, 6, 0:S], branch[:, NB + h, 0, :].bitcast(F32),
                                          ALU.subtract).then_inc(hb_lo, 1)
                for h in range(NA):
                    e = e_t[:, h % 2, :]
                    if H == p_mlstm(h) + 5:
                        dve.wait_ge(st_made, h + 1)
                        dve.scalar_tensor_tensor(out=e[:, 0:128], in0=ps[:, 4, 0:128], scalar=cols[:, 0, h:h + 1],
                                                 in1=late[:, :], op0=ALU.subtract, op1=ALU.max)
                        dve.scalar_tensor_tensor(out=e[:, 256:384], in0=ps[:, 4, 128:256], scalar=cols[:, 1, h:h + 1],
                                                 in1=late[:, :], op0=ALU.subtract, op1=ALU.max).then_inc(arg_made, 1)
                    if H == p_mlstm(h) + 7:
                        dve.wait_ge(e_made, h + 1)
                        dve.tensor_tensor(wt[:, h, :], e, ps[:, 7, 0:384], ALU.mult).then_inc(wt_made, 1)
                    if H == p_sv(h) + 5:
                        dve.wait_ge(num_kept, h + 1)
                        dve.tensor_copy(den[:, :, h], ps[:, 5:7, DV:DV + 1].rearrange("p m c -> p (m c)"))\
                           .then_inc(den_kept, 1)
                if H == p_sv(NA - 1) + 6:
                    dve.wait_ge(if_act, 5)
                    dve.wait_ge(den_kept, NA)
                    link(dve.scalar_tensor_tensor(out=den[:, :, :], in0=den[:, :, :], scalar=-1.0, in1=den[:, :, :],
                                                  op0=ALU.mult, op1=ALU.max))
                    link(dve.tensor_tensor(den[:, :, :], den[:, :, :], floor[:, :, :], ALU.max))
                    link(dve.reciprocal(den_r[:, :, :], den[:, :, :]))
                    link(dve.tensor_tensor(num_ss[:, :, :], num_ss[:, :, :], den_r[:, :, :], ALU.mult))
                    dve.tensor_tensor(num_ss[:, :, :], num_ss[:, :, :], den_r[:, :, :], ALU.mult).then_inc(hr_in, 1)
                if H == p_sv(NA - 1) + 8:
                    dve.wait_ge(hr_made, 1)
                    link(dve.tensor_tensor(h_fac[:, :, :], h_rms[:, :, :], den_r[:, :, :], ALU.mult))
                    for m in range(M):
                        for h in range(NA):
                            o = oa[:, m, DV * h:DV * h + DV]
                            last = dve.scalar_tensor_tensor(out=o, in0=num[:, m, h, :], scalar=h_fac[:, m, h:h + 1],
                                                            in1=o, op0=ALU.mult, op1=ALU.mult)
                    last.then_inc(ha_made, 1)
                if H == P_HA + 5:
                    dve.wait_ge(ha_hi, 1)
                    turned_lo(branch, range(8), 4, G_H).then_inc(ha_lo, 1)

            def gated_b(n):
                dve.wait_ge(w_used, 8 * (B_BRANCH + 3 * n) + 20)
                dve.wait_ge(kept[1], 7 + 2 * n)
                for m in range(M):
                    last = dve.tensor_tensor(gate[:, 1, m, :], gate[:, 1, m, :], ps[:, m, :], ALU.mult)
                last.then_inc(kept[0], 1)

            def gated_a(n):
                dve.wait_ge(w_used, 8 * (B_BRANCH + 3 * n) + 24)
                for m in range(M):
                    last = dve.tensor_tensor(gate[:, 0, m, :], gate[:, 0, m, :], ps[:, 2 + m, :], ALU.mult)
                last.then_inc(kept[1], 1)
                dve.wait_ge(kept[0], 8 + 2 * n)
                dve.wait_ge(kept[1], 8 + 2 * n)
                dve.tensor_tensor(gate_f[:, 0:1024], gate_f[:, 0:1024], gate_f[:, 1024:2048],
                                  ALU.add).then_inc(mg_made, 1)

            def merged_lo(n):
                dve.wait_ge(mg_hi, n + 1)
                mg = merged[:, bass.ds(4 * n, 4), :, :]
                dve.tensor_tensor(mg[:, :, 1, :], banks(4, 6).rearrange("p (t c) -> p t c", t=4),
                                  mg[:, :, 0, :].bitcast(F32), ALU.subtract).then_inc(mg_lo, 1)

            dve.memset(wif2[:, :].bitcast(F32), 0.0).then_inc(if_dve, 1)
            dve.wait_ge(g_turned, 1)
            dve.tensor_copy(g_col[:, 0:16], ps[:, 3, 0:16]).then_inc(g_kept, 1)
            dve.wait_ge(g_kept, 1)
            for k in range(8):
                dve.wait_ge(xh_made, k + 1)
                turned_lo(xT, (2 * k, 2 * k + 1), 4 + k % 4, G_MIX + 2 * k).then_inc(xl_made, 1)
                split_lo(0, k)
            for H in range(8, hn(1) + 8):
                jobs(H)
                if H == hn(0) + 24:
                    gated_b(0)
                if H == hn(0) + 28:
                    gated_a(0)
                if H == hn(0) + 31:
                    merged_lo(0)
                split_lo(H // 8, H % 8)
            with dve.Fori(1, NN) as n:
                for i in range(8, 32):
                    if i == 24:
                        gated_b(n)
                    if i == 28:
                        gated_a(n)
                    if i == 31:
                        merged_lo(n)
                    split_lo(B_BRANCH + 3 * n + i // 8, i % 8)
            for H in range(8 * B_OUT + 8, 8 * B_UP + 12):
                for i in range(NN):
                    if H == 8 * (B_OUT + i) + 12:
                        dve.wait_ge(w_used, 8 * (B_OUT + i) + 8)
                        dve.wait_ge(xr_landed, 16)
                        for m in range(M):
                            r = rows[:, m, N * i:N * i + N]
                            last = dve.tensor_tensor(r, r, ps[:, 2 * (i % 2) + m, :], ALU.add)
                        last.then_inc(kept[i % 2], 1)
                    if H == 8 * (B_OUT + i) + 15:
                        dve.wait_ge(x2_hi, i + 1)
                        turned_lo(xT, range(4 * i, 4 * i + 4), 4 if i < 3 else 0, G_MLP + 4 * i).then_inc(x2_lo, 1)
                if H == 8 * B_UP + 8:
                    dve.wait_ge(x2_summed, NN)
                    link(dve.tensor_reduce(x2_ms[:, :], x2_ss[:, :, :], AX, ALU.add))
                    link(dve.tensor_scalar(x2_ms[:, :], x2_ms[:, :], 1.0 / D, EPS, ALU.mult, ALU.add))
                    link(dve.reciprocal(x2_q[:, :], x2_ms[:, :]))
                split_lo(H // 8, H % 8)

            def add_down(f, n):
                for m in range(M):
                    if m == 0:
                        dve.wait_ge(down_m0, NN * f + n + 1)
                    else:
                        dve.wait_ge(w_used, 8 * (B_UP + FB * f + 8 + 2 * n) + 16)
                    r = rows[:, m, bass.ds(N * n, N)]
                    b = (4 + 2 * n) % 8 + m if isinstance(n, int) else 4 + 2 * n + m
                    dve.scalar_tensor_tensor(out=r, in0=ps[:, bass.ds(b, 1), :].rearrange("p a c -> p (a c)"),
                                             scalar=x2_q[:, m:m + 1], in1=r, op0=ALU.mult,
                                             op1=ALU.add).then_inc(down_read, 1)

            feats = [branch, merged]
            for f in range(2):
                blk0 = B_UP + FB * f
                for half in range(2):
                    feat = feats[half]
                    with dve.Fori(0, 2) as jj:
                        for u in range(2):
                            j = 4 * half + 2 * jj + u
                            q0 = 4 * ((u + 1) % 2)
                            dve.wait_ge(up_kept, 8 * f + j + 1)
                            dve.tensor_tensor(up_sq, ps[:, q0:q0 + 4, 0:S], up_lo, ALU.add).then_inc(up_read, 1)
                            dve.wait_ge(up_read, 8 * f + j + 1)
                            dve.scalar_tensor_tensor(out=up_sq, in0=up_sq, scalar=0.0, in1=up_sq, op0=ALU.max,
                                                     op1=ALU.mult).then_inc(up_squared, 1)
                            for i in range(12, 20):
                                if i == 14:
                                    dve.wait_ge(up_hi, 8 * f + j + 1)
                                    ft = feat[:, bass.ds(4 * (2 * jj + u), 4), :, :]
                                    dve.tensor_tensor(ft[:, :, 1, :], up_sq, ft[:, :, 0, :].bitcast(F32),
                                                      ALU.subtract).then_inc(up_lo_made, 1)
                                split_lo(blk0 + j + i // 8, i % 8)
                def down_splits(first, last):
                    for i in range(first, last):
                        split_lo(blk0 + 8 + i // 8, i % 8)

                down_splits(12, 20)
                for n in range(NN):
                    add_down(f, n)
                    down_splits(20 + 16 * n, min(36 + 16 * n, 76 if f == 0 else 64))

        @block.tensor
        def _(pe):
            def half_rows(blk, k, b0, feat, t0, start=False, stop=False, first_done=None):
                pe.wait_ge(lo_made, 8 * blk + k + 1)
                for m in range(M):
                    for i in range(KH):
                        t, s = t0 + i, k % RING
                        hi = feat[:, t, 0, P * m:P * m + P]
                        lo = feat[:, t, 1, P * m:P * m + P]
                        first, end = start and i == 0, stop and i == KH - 1
                        o = ps[:, b0 + m, :] if isinstance(b0, int) else \
                            ps[:, bass.ds(b0 + m, 1), :].rearrange("p a c -> p (a c)")
                        pe.matmul(o, hi, w_hi[:, s, i, :], start=first, stop=False)
                        pe.matmul(o, hi, w_lo[:, s, i, :], start=False, stop=False)
                        last = pe.matmul(o, lo, w_hi[:, s, i, :], start=False, stop=end)
                    if m == 0 and first_done is not None:
                        last.then_inc(first_done, 1)
                last.then_inc(w_used, 1)

            def half_cols(blk, k, q0):
                pe.wait_ge(lo_made, 8 * blk + k + 1)
                s = k % RING
                for i in range(KH):
                    t = KH * k + i
                    for j in range(4):
                        w = slice(P * j, P * j + P)

                        def by_lo():
                            return pe.matmul(ps[:, q0 + j, 0:S], w_lo[:, s, i, w], xT[:, t, 0, :], start=False,
                                             stop=False)

                        if t == KT - 1:
                            by_lo()
                        last = pe.matmul(ps[:, q0 + j, :], w_hi[:, s, i, w],
                                         xT[:, t, :, :].rearrange("p a c -> p (a c)"), start=t == 0, stop=t == KT - 1)
                        if t != KT - 1:
                            last = by_lo()
                last.then_inc(w_used, 1)

            def turn(dst_bank, col, src):
                r, c = src.shape
                return pe.transpose(ps[0:c, dst_bank, col:col + r], src, ident[0:r, 0:r])

            def turn_rows(b0, tiles, src, done):
                for i, t in enumerate(tiles):
                    for m in range(M):
                        last = turn(b0 + i // 2, S * (i % 2) + P * m, src[:, m, P * t:P * t + P])
                last.then_inc(done, 1)

            def turn_x(k):
                pe.wait_ge(x_landed[k], 16)
                if k >= 4:
                    pe.wait_ge(xl_made, k - 3)
                turn_rows(4 + k % 4, (2 * k, 2 * k + 1), rows, x_turned)

            def beside(p):
                if p == P_IF_SUM:
                    pe.wait_ge(if_lo, 1)
                    for t in range(KT):
                        last = pe.matmul(ps[:, 7, :], wif2[:, 16 * t:16 * t + P],
                                         xT[:, t, :, :].rearrange("p a c -> p (a c)"), start=t == 0, stop=t == KT - 1)
                    last.then_inc(if_pe, 1)
                if p == P_IF_ADD:
                    pe.wait_ge(if_act, 1)
                    pe.wait_ge(c_pool, 2)
                    for m in range(M):
                        for a in range(2):
                            last = pe.matmul(ps[:, 7, IF * m:IF * m + IF], if_raw[:, a, P * m:P * m + P], add2[:, :],
                                             start=a == 0, stop=a == 1)
                    last.then_inc(if_pe, 1)
                if p == P_IF_ROWS:
                    pe.wait_ge(if_dve, 2)
                    pe.wait_ge(qk_kept, 2)
                    for a in range(2):
                        for m in range(M):
                            last = turn(7, S * a + P * m, if_nat[:, m, NA * a:NA * a + NA])
                    last.then_inc(if_pe, 1)
                if p == P_IF_COLS:
                    pe.wait_ge(if_dve, 5)
                    pe.wait_ge(qk_kept, 4)
                    for i, r in enumerate((a_r[:, 0:L], a_r[:, L:S], lw_r[:, :], m_r[:, 0:L], m_r[:, L:S])):
                        last = turn(7, NA * i, r)
                    last.then_inc(if_pe, 1)
                for i in range(4):
                    if p == 8 * i + 12:
                        pe.wait_ge(nat_scaled, i + 1)
                        if i == 1:
                            pe.wait_ge(if_dve, 2)
                        if i == 2:
                            pe.wait_ge(qk_kept, 1)
                        if i == 3:
                            pe.wait_ge(qk_kept, 2)
                            pe.wait_ge(if_dve, 3)
                        turn_rows(4 + 2 * (i % 2), range(4), nat[i % 2], qk_turned)
                    if p == 60 + 5 * i:
                        b = 6 + i // 2
                        pe.wait_ge(kept[b % 2], b // 2 + 1)
                        pe.wait_ge(qk_kept, 4 + i)
                        if i == 0:
                            pe.wait_ge(if_dve, 6)
                        turn_rows(7, range(2 * (i % 2), 2 * (i % 2) + 2), nat[b % 2], qk_turned)
                for h in range(NB):
                    if p == p_moba(h):
                        pe.wait_ge(qk_kept, 4)
                        if h >= 1:
                            pe.wait_ge(low_made, h)
                        pe.matmul(ps[:, 4, 0:128], qTb[:, h, 0:128], kTb[:, h, 0:128], start=True, stop=True)
                        pe.matmul(ps[:, 4, 128:384], qTb[:, h, 128:256], kTb[:, h, :], start=True,
                                  stop=True).then_inc(sc_made, 1)
                    if p == p_moba(h) + 7:
                        pe.wait_ge(p_scaled, h + 1)
                        if h >= 1:
                            pe.wait_ge(pt_kept, h)
                        for i in range(3):
                            last = turn(5, P * i, prob[:, h % 2, P * i:P * i + P])
                        last.then_inc(p_turned, 1)
                    if p == p_moba(h) + 13:
                        pe.wait_ge(pt_kept, h + 1)
                        if h == 0:
                            pe.wait_ge(kept[0], 3)
                            pe.wait_ge(kept[1], 3)
                        else:
                            pe.wait_ge(hb_lo, h)
                        v0, v1 = (vb[:, m, DH * h:DH * h + DH] for m in range(M))
                        pt = probT[:, h % 2, :]
                        pe.matmul(ps[:, 6, 0:128], v0, pt[:, 0:128], start=True, stop=True)
                        pe.matmul(ps[:, 6, 128:256], v0, pt[:, 128:256], start=True, stop=False)
                        pe.matmul(ps[:, 6, 128:256], v1, pt[:, 256:384], start=False, stop=True).then_inc(hb_made, 1)
                for h in range(NA):
                    if p == p_mlstm(h):
                        if h == 0:
                            pe.wait_ge(qk_kept, 8)
                            pe.wait_ge(if_dve, 6)
                            pe.wait_ge(low_made, NB)
                        else:
                            pe.wait_ge(wt_made, h)
                        pe.matmul(ps[:, 7, 0:256], kTa[:, h, 0:128], qTa[:, h, :], start=True, stop=True)
                        pe.matmul(ps[:, 7, 256:384], kTa[:, h, 128:256], qTa[:, h, 128:256], start=True, stop=True)
                        pe.matmul(ps[:, 4, 0:S], pick[:, h, :], g_r[:, :], start=True, stop=True).then_inc(st_made, 1)
                    if p == p_sv(h):
                        pe.wait_ge(wt_made, h + 1)
                        if h == 0:
                            pe.wait_ge(kept[0], 5)
                            pe.wait_ge(kept[1], 5)
                            pe.wait_ge(pt_kept, NB)
                            pe.wait_ge(hb_lo, NB)
                        else:
                            pe.wait_ge(den_kept, h)
                        for c, w, v in ((0, DV, va[:, :, DV * h:DV * h + DV]), (DV, 2, None)):
                            v0, v1 = (v[:, 0, :], v[:, 1, :]) if v is not None else (ones[:, :], ones[:, :])
                            pe.matmul(ps[:, 5, c:c + w], wt[:, h, 0:128], v0, start=True, stop=True)
                            pe.matmul(ps[:, 6, c:c + w], wt[:, h, 128:256], v0, start=True, stop=False)
                            last = pe.matmul(ps[:, 6, c:c + w], wt[:, h, 256:384], v1, start=False, stop=True)
                        last.then_inc(sv_made, 1)
                if p == P_HA:
                    pe.wait_ge(ha_made, 1)
                    turn_rows(4, range(8), oa, ha_turned)

            pe.wait_ge(c_pool, 1)

            def keep_warm(n):
                for _ in range(n):
                    pe.matmul(ps[:, 2, 0:P], ident[:, :], ident[:, :], start=True, stop=True)

            keep_warm(8)
            pe.wait_ge(mix_landed, 16)
            turn(3, 0, mix_rows[:, :]).then_inc(g_turned, 1)
            turn_x(0)
            turn_x(1)
            keep_warm(12)
            for b in range(N_WIN):
                if b >= 2:
                    pe.wait_ge(kept[b % 2], b // 2)
                elif b == 1:
                    pe.wait_ge(g_kept, 2)
                for k in range(8):
                    if b == 0:
                        pe.wait_ge(xl_made, k + 1)
                    half_rows(b, k, 2 * (b % 2), xT, 2 * k, start=k == 0, stop=k == 7)
                    if b == 0 and k < 6:
                        turn_x(k + 2)
                    if b == 0 and k == 4:
                        pe.wait_ge(c_landed, 16 * 6)
                        pe.wait_ge(g_kept, 1)
                        turn(3, 16, g_rows[:, :]).then_inc(g_turned, 1)
                    beside(8 * b + k)


            def branch_block(n, after):
                blk = B_BRANCH + 3 * n
                for a in range(2):
                    pe.wait_ge(kept[a], 6 + 2 * n)
                    for k in range(8):
                        half_rows(blk + a, k, 2 * a, xT, 2 * k, start=k == 0, stop=k == 7)
                        after(8 * a + k)
                for k in range(8):
                    a = k // 4
                    if k % 4 == 0:
                        pe.wait_ge(kept[a], 7 + 2 * n)
                        if isinstance(n, int):
                            pe.wait_ge((hb_lo, ha_lo)[a], (NB, 1)[a])
                    half_rows(blk + 2, k, 2 * a, branch, 2 * (k % 4) + (8, 0)[a], start=k % 4 == 0, stop=k % 4 == 3)
                    after(16 + k)

            def turn_merged(n):
                pe.wait_ge(mg_made, n + 1)
                turn_rows(4, range(4), gate[:, 0, :, :], mg_turned)

            def turn_x2(i):
                pe.wait_ge(kept[i % 2], 15 + i // 2)
                if i in (1, 2):
                    pe.wait_ge(x2_lo, i)
                if i == 3:
                    pe.wait_ge(kept[0], 16)
                turn_rows(4 if i < 3 else 0, range(4 * i, 4 * i + 4), rows, x2_turned)

            branch_block(0, lambda i: beside(hn(0) + i))
            with pe.Fori(1, NN) as n:
                branch_block(n, lambda i: turn_merged(n - 1) if i == 2 else None)
            for i in range(NN):
                pe.wait_ge(kept[i % 2], 14 + i // 2)
                for k in range(8):
                    if i == 0 and k % 2 == 0:
                        pe.wait_ge(mg_lo, k // 2 + 1)
                    half_rows(B_OUT + i, k, 2 * (i % 2), merged, 2 * k, start=k == 0, stop=k == 7)
                    if k == 2:
                        turn_merged(NN - 1) if i == 0 else turn_x2(i - 1)
            for f in range(2):
                blk0 = B_UP + FB * f
                for j in range(2):
                    if f == 1:
                        pe.wait_ge(down_read, M * 2 * (j + 1))
                    elif j == 1:
                        pe.wait_ge(kept[0], 16)
                        pe.wait_ge(kept[1], 16)
                    for k in range(8):
                        if f == 0 and j == 0 and k in (0, 6):
                            pe.wait_ge(x2_lo, 3 + k // 6)
                        half_cols(blk0 + j, k, 4 * ((j + 1) % 2))
                        if f == 0 and j == 0 and k == 2:
                            turn_x2(3)
                with pe.Fori(1, 4) as jj:
                    for u in range(2):
                        pe.wait_ge(up_read, 8 * f + 2 * jj + u - 1)
                        for k in range(8):
                            half_cols(blk0 + 2 * jj + u, k, 4 * ((u + 1) % 2))
                for pair in range(2):
                    pe.wait_ge(up_read, 8 * f + 7 + pair)
                    with pe.Fori(0, 2) as n:
                        for i in range(16):
                            if pair == 0 and i % 2 == 0:
                                pe.wait_ge(up_lo_made, 8 * f + i // 2 + 1)
                            half_rows(blk0 + 8 + 4 * pair + 2 * n + i // 8, i % 8, 4 * (1 - pair) + 2 * n,
                                      branch if i < 8 else merged, 2 * (i % 8), start=i == 0, stop=i == 15,
                                      first_done=down_m0 if i == 15 else None)


_INS = ['x', 'norm_mix', 'w_in', 'b_if', 'norm_h_mlstm', 'norm_q_moba', 'norm_k_moba', 'w_branch_a', 'w_branch_b',
        'w_out', 'norm_mlp', 'w_up', 'w_down']
_OUTS = [((1, S, D), 'float32')]


def kernel(**inputs):
    import numpy as _np
    import concourse.bacc as _bacc
    from concourse import mybir as _mybir
    from concourse.bass_utils import run_bass_kernel_spmd as _run

    nc = _bacc.Bacc("TRN2", target_bir_lowering=False, num_devices=1)
    arrays, args = {}, []
    for name in _INS:
        a = _np.ascontiguousarray(inputs[name])
        arrays[f"in_{name}_dram"] = a
        args.append(nc.dram_tensor(f"in_{name}_dram", a.shape, _mybir.dt.from_np(a.dtype), kind="ExternalInput").ap())
    for i, (shape, dtype) in enumerate(_OUTS):
        dt = _mybir.dt.from_np(_np.dtype(dtype))
        args.append(nc.dram_tensor(f"out_{i}_dram", shape, dt, kind="ExternalOutput").ap())
    build(nc, *args)
    r = _run(nc, [arrays], core_ids=[0])
    got = tuple(r.results[0][f"out_{i}_dram"] for i in range(len(_OUTS)))
    return got[0]
```
